# Optimizing a Trainium2 kernel written in Bass

```python
import jax, jax.numpy as jnp
from jax import lax
import numpy as np

D_MODEL = 1024
BATCH = 1
SEQ = 1024
DEPTH = 2
DEC_BATCH = 8
DEC_SEQ = 1
PAST_LEN = 4096
PAGE_SIZE = 128

N_A_LAYERS = DEPTH // 2
N_B_LAYERS = DEPTH - N_A_LAYERS
HG_HEAD_K = 128
HG_HEADS = D_MODEL // HG_HEAD_K
HG_HEAD_V = D_MODEL // HG_HEADS
HG_KEY_DIM = HG_HEADS * HG_HEAD_K
HG_VAL_DIM = HG_HEADS * HG_HEAD_V
HG_CHUNK = 64
ATT_HEAD_DIM = 64
ATT_Q_HEADS = D_MODEL // ATT_HEAD_DIM
ATT_KV_HEADS = max(1, ATT_Q_HEADS // 8)
ATT_GROUP = ATT_Q_HEADS // ATT_KV_HEADS
ATT_Q_DIM = ATT_Q_HEADS * ATT_HEAD_DIM
WINDOW = 128
ATT_BLOCK = WINDOW
ROPE_THETA = 500000.0
ROT_DIM = ATT_HEAD_DIM // 4
NORM_EPS = 1e-6
MASK_VALUE = -1e30

kernel_name = 'yoco_hgrn2_swa_sink_decode_step'

F32 = jnp.float32

def _rmsnorm(x, g):
    xf = x.astype(F32)
    r = lax.rsqrt(jnp.mean(xf * xf, axis=-1, keepdims=True) + NORM_EPS)
    return (xf * r * g.astype(F32)).astype(x.dtype)

def _rope(x, pos):
    half = ROT_DIM // 2
    inv_freq = 1.0 / (ROPE_THETA ** (jnp.arange(half, dtype=F32) * 2.0 / ROT_DIM))
    ang = pos.astype(F32)[:, None] * inv_freq[None, :]
    cos = jnp.cos(ang)[None, :, None, :]
    sin = jnp.sin(ang)[None, :, None, :]
    xf = x.astype(F32)
    x1, x2, rest = xf[..., :half], xf[..., half:ROT_DIM], xf[..., ROT_DIM:]
    out = jnp.concatenate([x1 * cos - x2 * sin, x2 * cos + x1 * sin, rest], axis=-1)
    return out.astype(x.dtype)

def _chunked_gated_recurrence(q, k, v, log_f, s0):
    B, T, H, _ = q.shape
    dv = v.shape[-1]
    C = min(HG_CHUNK, T)
    pad = (-T) % C
    n = (T + pad) // C

    def blocks(a):
        a = jnp.pad(a, ((0, 0), (0, pad), (0, 0), (0, 0)))
        return a.reshape(B, n, C, H, a.shape[-1]).transpose(1, 0, 3, 2, 4)

    causal = jnp.tril(jnp.ones((C, C), dtype=bool))[:, :, None]

    def step(S, inp):
        qc, kc, vc, lc = inp
        b = jnp.cumsum(lc, axis=2)
        o = jnp.einsum('bhtd,bhde->bhte', qc * jnp.exp(b), S)
        diff = b[:, :, :, None, :] - b[:, :, None, :, :]
        decay = jnp.where(causal, jnp.exp(jnp.where(causal, diff, 0.0)), 0.0)
        a = jnp.einsum('bhtd,bhsd,bhtsd->bhts', qc, kc, decay)
        o = o + jnp.einsum('bhts,bhse->bhte', a, vc)
        b_end = b[:, :, -1:, :]
        S = (jnp.exp(b_end[:, :, 0, :])[..., None] * S
             + jnp.einsum('bhsd,bhse->bhde', kc * jnp.exp(b_end - b), vc))
        return S, o

    s_fin, o = lax.scan(step, s0, (blocks(q), blocks(k), blocks(v), blocks(log_f)))
    o = o.transpose(1, 0, 3, 2, 4).reshape(B, n * C, H, dv)[:, :T]
    return o, s_fin

def _hgrn2_layer(h, s0, norm_g, w_in, lb, gnorm, w_out):
    B, T, _ = h.shape
    u = _rmsnorm(h, norm_g) @ w_in
    q, f, i, g = jnp.split(u, [HG_KEY_DIM, 2 * HG_KEY_DIM, 2 * HG_KEY_DIM + HG_VAL_DIM], axis=-1)
    q = jax.nn.silu(q.astype(F32)).reshape(B, T, HG_HEADS, HG_HEAD_K)
    f = f.astype(F32).reshape(B, T, HG_HEADS, HG_HEAD_K)
    lb = lb.astype(F32).reshape(HG_HEADS, HG_HEAD_K)
    log_f = jax.nn.log_sigmoid(f) + jnp.log1p(lb * jnp.exp(-f))
    k = (1.0 - lb) * jax.nn.sigmoid(-f)
    v = i.astype(F32).reshape(B, T, HG_HEADS, HG_HEAD_V)
    o, s_new = _chunked_gated_recurrence(q, k, v, log_f, s0.astype(F32))
    o = _rmsnorm(o, gnorm).reshape(B, T, HG_VAL_DIM)
    y = (o * jax.nn.silu(g.astype(F32))).astype(h.dtype) @ w_out
    return h + y, s_new.astype(s0.dtype)

def _shared_kv(h, kv_norm, w_kv, pos):
    B, T, _ = h.shape
    u = _rmsnorm(h, kv_norm) @ w_kv
    k, v = jnp.split(u, 2, axis=-1)
    k = _rope(k.reshape(B, T, ATT_KV_HEADS, ATT_HEAD_DIM), pos)
    v = v.reshape(B, T, ATT_KV_HEADS, ATT_HEAD_DIM)
    return k, v

def _sink_attention(q, k, v, mask, sinks):
    scale = ATT_HEAD_DIM ** -0.5
    s = jnp.einsum('bnqkgd,bnskd->bnkgqs', q.astype(F32), k.astype(F32)) * scale
    valid = mask[None, :, None, None]
    s = jnp.where(valid, s, MASK_VALUE)
    sink = sinks.astype(F32)[None, None, :, :, None, None]
    m = jnp.maximum(jnp.max(s, axis=-1, keepdims=True), sink)
    p = jnp.where(valid, jnp.exp(s - m), 0.0)
    denom = jnp.sum(p, axis=-1, keepdims=True) + jnp.exp(sink - m)
    return jnp.einsum('bnkgqs,bnskd->bnqkgd', p / denom, v.astype(F32))

def _swa_layer(h, k, v, pos, past_k, past_v, norm_g, w_in, sinks, w_out):
    B, T, _ = h.shape
    u = _rmsnorm(h, norm_g) @ w_in
    q, gate = jnp.split(u, [ATT_Q_DIM], axis=-1)
    q = _rope(q.reshape(B, T, ATT_Q_HEADS, ATT_HEAD_DIM), pos)
    q = q.reshape(B, T, ATT_KV_HEADS, ATT_GROUP, ATT_HEAD_DIM)
    sinks_g = sinks.reshape(ATT_KV_HEADS, ATT_GROUP)
    if past_k is None:
        nb = T // ATT_BLOCK
        qb = q.reshape(B, nb, ATT_BLOCK, ATT_KV_HEADS, ATT_GROUP, ATT_HEAD_DIM)

        def band(a):
            ab = a.reshape(B, nb, ATT_BLOCK, ATT_KV_HEADS, ATT_HEAD_DIM)
            prev = jnp.concatenate([jnp.zeros_like(ab[:, :1]), ab[:, :-1]], axis=1)
            return jnp.concatenate([prev, ab], axis=2)

        tq = jnp.arange(ATT_BLOCK)[:, None]
        j = jnp.arange(2 * ATT_BLOCK)[None, :]
        rel = tq + ATT_BLOCK - j
        mask = ((rel >= 0) & (rel <= WINDOW))[None]
        mask = mask & ((jnp.arange(nb)[:, None, None] > 0) | (j[None] >= ATT_BLOCK))
        o = _sink_attention(qb, band(k), band(v), mask, sinks_g)
    else:
        w = past_k.shape[1]
        kk = jnp.concatenate([past_k.astype(k.dtype), k], axis=1)[:, None]
        vv = jnp.concatenate([past_v.astype(v.dtype), v], axis=1)[:, None]
        kpos = jnp.concatenate([pos[0] - w + jnp.arange(w, dtype=pos.dtype), pos])
        rel = pos[:, None] - kpos[None, :]
        mask = ((rel >= 0) & (rel <= WINDOW))[None]
        o = _sink_attention(q[:, None], kk, vv, mask, sinks_g)
    o = o.reshape(B, T, ATT_Q_DIM)
    y = (o * jax.nn.silu(gate.astype(F32))).astype(h.dtype) @ w_out
    return h + y

def _trunk(x, pos, s0, past_k, past_v, a_norm, a_w_in, a_lb_logits, a_gnorm, a_w_out,
           kv_norm, w_kv, b_norm, b_w_in, b_sinks, b_w_out, final_norm):
    p = jax.nn.softmax(a_lb_logits.astype(F32), axis=0)
    lbs = jnp.cumsum(p, axis=0) - p[0:1]
    h = x
    new_states = []
    k = v = None
    for layer in range(DEPTH):
        if layer < N_A_LAYERS:
            h, s = _hgrn2_layer(h, s0[layer], a_norm[layer], a_w_in[layer], lbs[layer],
                                a_gnorm[layer], a_w_out[layer])
            new_states.append(s)
        else:
            if layer == N_A_LAYERS:
                k, v = _shared_kv(h, kv_norm, w_kv, pos)
            j = layer - N_A_LAYERS
            h = _swa_layer(h, k, v, pos, past_k, past_v, b_norm[j], b_w_in[j], b_sinks[j], b_w_out[j])
    return _rmsnorm(h, final_norm), jnp.stack(new_states), k, v

def setup_inputs(seed: int = 0) -> dict:
    key = jax.random.key(seed)
    ks = jax.random.split(key, 20)
    D = D_MODEL
    w_rows = min(WINDOW, PAST_LEN)
    a_in = 2 * HG_KEY_DIM + 2 * HG_VAL_DIM
    b_in = 2 * ATT_Q_DIM
    kv_out = 2 * ATT_KV_HEADS * ATT_HEAD_DIM
    nrm = jax.random.normal
    return {
        'x_prompt': nrm(ks[0], (BATCH, SEQ, D), F32),
        'x_sample': nrm(ks[1], (DEC_BATCH, DEC_SEQ, D), F32),
        'state_hgrn': 0.5 * nrm(ks[2], (N_A_LAYERS, DEC_BATCH, HG_HEADS, HG_HEAD_K, HG_HEAD_V), F32),
        'cache_k_win': nrm(ks[3], (DEC_BATCH, w_rows, ATT_KV_HEADS, ATT_HEAD_DIM), F32),
        'cache_v_win': nrm(ks[4], (DEC_BATCH, w_rows, ATT_KV_HEADS, ATT_HEAD_DIM), F32),
        'a_norm': 1.0 + 0.05 * nrm(ks[5], (N_A_LAYERS, D), F32),
        'a_w_in': nrm(ks[6], (N_A_LAYERS, D, a_in), F32) * D ** -0.5,
        'a_lb_logits': nrm(ks[7], (N_A_LAYERS, HG_KEY_DIM), F32),
        'a_gnorm': 1.0 + 0.05 * nrm(ks[8], (N_A_LAYERS, HG_HEAD_V), F32),
        'a_w_out': nrm(ks[9], (N_A_LAYERS, HG_VAL_DIM, D), F32) * HG_VAL_DIM ** -0.5,
        'kv_norm': 1.0 + 0.05 * nrm(ks[10], (D,), F32),
        'w_kv': nrm(ks[11], (D, kv_out), F32) * D ** -0.5,
        'b_norm': 1.0 + 0.05 * nrm(ks[12], (N_B_LAYERS, D), F32),
        'b_w_in': nrm(ks[13], (N_B_LAYERS, D, b_in), F32) * D ** -0.5,
        'b_sinks': nrm(ks[14], (N_B_LAYERS, ATT_Q_HEADS), F32),
        'b_w_out': nrm(ks[15], (N_B_LAYERS, ATT_Q_DIM, D), F32) * ATT_Q_DIM ** -0.5,
        'final_norm': 1.0 + 0.05 * nrm(ks[16], (D,), F32),
    }

def reference(x_prompt, x_sample, state_hgrn, cache_k_win, cache_v_win, a_norm, a_w_in,
              a_lb_logits, a_gnorm, a_w_out, kv_norm, w_kv, b_norm, b_w_in, b_sinks,
              b_w_out, final_norm):
    bp, tp, _ = x_prompt.shape
    ts = x_sample.shape[1]
    s0_prompt = jnp.zeros((N_A_LAYERS, bp, HG_HEADS, HG_HEAD_K, HG_HEAD_V), x_prompt.dtype)
    pos_p = jnp.arange(tp, dtype=jnp.int32)
    pos_s = PAST_LEN + jnp.arange(ts, dtype=jnp.int32)
    y_prompt, st_p, k_p, v_p = _trunk(x_prompt, pos_p, s0_prompt, None, None,
                                      a_norm, a_w_in, a_lb_logits, a_gnorm, a_w_out,
                                      kv_norm, w_kv, b_norm, b_w_in, b_sinks, b_w_out, final_norm)
    y_sample, st_s, k_s, v_s = _trunk(x_sample, pos_s, state_hgrn, cache_k_win, cache_v_win,
                                      a_norm, a_w_in, a_lb_logits, a_gnorm, a_w_out,
                                      kv_norm, w_kv, b_norm, b_w_in, b_sinks, b_w_out, final_norm)
    w_keep = min(WINDOW, tp)
    return (y_prompt, y_sample, st_p, st_s, k_p[:, -w_keep:], v_p[:, -w_keep:], k_s, v_s)


_drawn_inputs = setup_inputs


def setup_inputs(seed=0):
    import zlib

    import numpy as np

    out = dict(_drawn_inputs(seed))
    spreads = {}
    factors = {'b_norm': 8.0, 'b_sinks': 8.0}
    for name, (base, spread) in spreads.items():
        noise = np.random.default_rng([zlib.crc32(name.encode()), seed]).standard_normal(out[name].shape)
        drawn = base * np.exp(spread * noise) if base else spread * noise
        out[name] = __import__('jax').numpy.asarray(drawn.astype(out[name].dtype))
    for name, factor in factors.items():
        out[name] = (out[name] * factor).astype(out[name].dtype)
    return out
```

```python
from contextlib import ExitStack

import concourse.bass as bass
from concourse import mybir

D = 1024
P = 128
KT = D // P
SEQ, DEC = 1024, 8
T = SEQ + DEC
NU = 3
TU = T // NU
HEADS = 8
NC = SEQ // P
LEVELS = (64, 32, 16, 8, 4, 2, 1)
NL = len(LEVELS)
HP = 8
EPS = 1e-6
MASKED = -1e30
N_G = 3 * HEADS
N_AO = N_G + HEADS
N_KV = N_AO + KT
N_BQ = N_KV + 2
N_BG = N_BQ + HP
N_BO = N_BG + HP
NBLK = N_BO + KT
GAIN_A, GAIN_O, GAIN_KV, GAIN_B, GAIN_F = range(5)

GROUPS = ([("VT0", "act"), ("VT1", "act"), ("D0", "dve"), ("D1", "dve")]
          + [(f"L{h}", "dve") for h in LEVELS]
          + [("T0", "act"), ("T1", "act"), ("VB0", "dve"), ("VB1", "dve"), ("S0", "state"), ("S1", "state"),
             ("O0", "dve"), ("O1", "dve"), ("OS", "dve"), ("N0", "act"), ("N1", "act"), ("N2", "act")])
NGROUP = len(GROUPS)
GINDEX = {name: i for i, (name, _) in enumerate(GROUPS)}
NBANK_R = 5
READS = {e: [n for n, who in GROUPS if who == e] for e in ("act", "dve")}


def build(nc, ctx, ins, outs):
    fp32, fp32r, bf16, u8 = mybir.dt.float32, mybir.dt.float32r, mybir.dt.bfloat16, mybir.dt.uint8
    ALU, ACT = mybir.AluOpType, mybir.ActivationFunctionType
    AX = mybir.AxisListType
    x_d, w_d, gain_d, lbl_d, st_d, lmask_d, ident_d, cs_d, amask_d, smask_d, sink_d, sinks_d, kc_d, vc_d = ins
    y_d, stp_d, sts_d, kwin_d, vwin_d = outs
    h1_d = nc.dram_tensor("h1_spill", [P, KT, T], fp32, kind="Internal").ap()
    sg_d = nc.dram_tensor("gate_spill", [P, HP, T], fp32, kind="Internal").ap()

    base = (nc.sbuf_base + 31) // 32 * 32
    at = [base]
    size = {fp32: 4, fp32r: 4, bf16: 2, u8: 1}

    def sb(name, shape, dt, cursor=at):
        n = size[dt]
        for s in shape[1:]:
            n *= s
        t = nc.alloc_sbuf_tensor_at(name, shape, dt, offset=cursor[0])
        cursor[0] += (n + 31) // 32 * 32
        assert cursor[0] <= nc.sbuf_top, (name, cursor[0])
        return t

    XH, XL = sb("XH", [P, KT, T], fp32r), sb("XL", [P, KT, T], fp32r)
    A = sb("A", [P, KT, T], fp32)
    WR = sb("WR", [P, 3, KT, P], fp32)
    WH, WL = sb("WH", [P, 3, KT, P], fp32r), sb("WL", [P, 3, KT, P], fp32r)
    RB = sb("RB", [P, T], fp32)
    ones = sb("ones", [P, P], fp32)
    ident = sb("ident", [P, P], fp32)
    gain = sb("gain", [P, 5, KT], fp32)
    eps = sb("eps", [P, 1], fp32)
    spare = sb("spare", [P, 1], fp32)
    tick = sb("tick", [P, 1], fp32)
    rest = at[0]

    ra = [rest]
    RAWV, RAWF, RAWQ = (sb(n, [P, T], fp32, ra) for n in ("RAWV", "RAWF", "RAWQ"))
    TA = sb("TA", [P, T], fp32, ra)
    B = sb("B", [P, T], fp32, ra)
    K, Q = sb("K", [P, T], fp32, ra), sb("Q", [P, T], fp32, ra)
    X = [sb(f"X{i}", [P, T], fp32, ra) for i in range(3)]
    QE = sb("QE", [P, NC, P], fp32, ra)
    AT = sb("AT", [P, NC, P], fp32, ra)
    VH = sb("VH", [P, NC, P], fp32, ra)
    ST = sb("ST", [P, NC, P], fp32, ra)
    SS = sb("SS", [P, DEC, P], fp32, ra)
    VS = sb("VS", [P, DEC], fp32, ra)
    DEC_C = sb("DEC_C", [P, NC + DEC], fp32, ra)
    lmask = sb("lmask", [P, NL, P // 2], u8, ra)
    imask = sb("imask", [P, P], u8, ra)
    carry = sb("carry", [P, T], bf16, ra)
    lbw = sb("lbw", [P, 4, HEADS], fp32, ra)
    lb2 = sb("lb2", [P, HEADS, 2], fp32, ra)
    lbh = sb("lbh", [P, 2], fp32, ra)

    rb_ = [rest]
    KBH, KBL = sb("KBH", [P, 2, SEQ], fp32r, rb_), sb("KBL", [P, 2, SEQ], fp32r, rb_)
    VPH, VPL = sb("VPH", [P, NC, 192], fp32r, rb_), sb("VPL", [P, NC, 192], fp32r, rb_)
    EV, EV2 = sb("EV", [P, T], fp32, rb_), sb("EV2", [P, T], fp32, rb_)
    RES = [sb(f"RES{i}", [P, T], fp32, rb_) for i in range(2)]
    amask = sb("amask", [P, 2 * P], fp32, rb_)
    sink = sb("sink", [P, 16], fp32, rb_)
    smask = sb("smask", [P, DEC], fp32, rb_)
    sinks = sb("sinks", [P, 1], fp32, rb_)
    small = sb("small", [P, 2, 6, 4], fp32, rb_)
    dsm = sb("dsm", [P, 6], fp32, rb_)
    KSN = sb("KSN", [P, DEC], fp32, rb_)
    rc = [rb_[0]]
    CS = sb("CS", [P, 2, T], fp32, rc)
    VN = sb("VN", [DEC, P], fp32, rc)
    rd = [rb_[0]]
    re_ = [rest]
    SQ = sb("SQ", [P, T], fp32, re_)
    SQA = sb("SQA", [P, T], fp32, re_)
    QNH, QNL = sb("QNH", [P, HP, P], fp32r, rd), sb("QNL", [P, HP, P], fp32r, rd)
    PTH, PTL = sb("PTH", [P, 2, 512], fp32r, rd), sb("PTL", [P, 2, 512], fp32r, rd)
    SP_ = [sb(f"SP{i}", [P, 4, 256], fp32, rd) for i in range(2)]
    rs = [rb_[0]]
    SST = sb("SST", [P, P], fp32, rs)
    SSN = sb("SSN", [P, P + DEC], fp32, rs)
    PST = sb("PST", [P, P], fp32, rs)
    PSN = sb("PSN", [DEC, P], fp32, rs)
    QS = sb("QS", [P, DEC, 2, HP], fp32, rs)

    G = [ctx.enter_context(nc.psum_tensor(f"G{i}", [P, 512], fp32)) for i in range(3)]
    R = [ctx.enter_context(nc.psum_tensor(f"R{i}", [P, 512], fp32)) for i in range(NBANK_R)]

    def sem(name):
        return ctx.enter_context(nc.semaphore(name))

    const_in = sem("const_in")
    lbl_diff = sem("lbl_diff")
    lbl_exp = sem("lbl_exp")
    lb_done = sem("lb_done")
    head_lb = sem("head_lb")
    masks_done = sem("masks_done")
    x_split = sem("x_split")
    sq_done = sem("sq_done")
    sq_used = sem("sq_used")
    ln_done = sem("ln_done")
    rb_done = sem("rb_done")
    raw_in0 = sem("raw_in0")
    raw_in1 = sem("raw_in1")
    raw_in2 = sem("raw_in2")
    gained = sem("gained")
    hi_done = sem("hi_done")
    lo_done = sem("lo_done")
    unit_done = sem("unit_done")
    unit_read = sem("unit_read")
    group_done = sem("group_done")
    read_dve = sem("read_dve")
    read_act = sem("read_act")
    f_soft = sem("f_soft")
    b_log = sem("b_log")
    k_log = sem("k_log")
    k_exp = sem("k_exp")
    lb_ln = sem("lb_ln")
    k_done = sem("k_done")
    b_add = sem("b_add")
    b_scan = sem("b_scan")
    q_soft = sem("q_soft")
    q_log = sem("q_log")
    q_sig = sem("q_sig")
    q_done = sem("q_done")
    vs_done = sem("vs_done")
    dec_done = sem("dec_done")
    dif_done = sem("dif_done")
    dif_exp = sem("dif_exp")
    level_done = sem("level_done")
    qe_exp = sem("qe_exp")
    qe_done = sem("qe_done")
    ke_done = sem("ke_done")
    vd_done = sem("vd_done")
    ss_in = sem("ss_in")
    ss_decayed = sem("ss_decayed")
    ss_done = sem("ss_done")
    st_step = sem("st_step")
    osq_done = sem("osq_done")
    rn_done = sem("rn_done")
    head_done = sem("head_done")
    stp_out = sem("stp_out")
    sts_out = sem("sts_out")
    setup_dve = sem("setup_dve")
    act_link = sem("act_link")
    g_soft = sem("g_soft")
    g_log = sem("g_log")
    g_sig = sem("g_sig")
    g_silu = sem("g_silu")
    g_done = sem("g_done")
    cut_hi = sem("cut_hi")
    cut_lo = sem("cut_lo")
    res_in0 = sem("res_in0")
    res_in1 = sem("res_in1")
    h1_out = sem("h1_out")
    sq1_done = sem("sq1_done")
    sq1_added = sem("sq1_added")
    sums1_done = sem("sums1_done")
    ln1_done = sem("ln1_done")
    rb1_done = sem("rb1_done")
    const2_in = sem("const2_in")
    k_rot = sem("k_rot")
    k_out = sem("k_out")
    kb_zero = sem("kb_zero")
    kb_high = sem("kb_high")
    kb_done = sem("kb_done")
    v_raw = sem("v_raw")
    v_out = sem("v_out")
    v_turned = sem("v_turned")
    vp_high = sem("vp_high")
    vp_done = sem("vp_done")
    vn_done = sem("vn_done")
    q_raw = sem("q_raw")
    q_shuffled = sem("q_shuffled")
    q_cos = sem("q_cos")
    q_sin = sem("q_sin")
    q_rot = sem("q_rot")
    cache_in = sem("cache_in")
    d_qs = sem("d_qs")
    d_scores = sem("d_scores")
    d_copied = sem("d_copied")
    d_turned = sem("d_turned")
    d_max = sem("d_max")
    d_exp = sem("d_exp")
    d_prob = sem("d_prob")
    d_ptur = sem("d_ptur")
    d_pcop = sem("d_pcop")
    d_out = sem("d_out")
    d_done = sem("d_done")
    dve_small = sem("dve_small")
    gate_soft = sem("gate_soft")
    gate_log = sem("gate_log")
    gate_sig = sem("gate_sig")
    gate_silu = sem("gate_silu")
    sg_out = sem("sg_out")
    sg_in0 = sem("sg_in0")
    sg_in1 = sem("sg_in1")
    gated = sem("gated")
    qn_high = sem("qn_high")
    qn_done = sem("qn_done")
    sc_done = sem("sc_done")
    sc_read = sem("sc_read")
    m_ready = sem("m_ready")
    p_exp = sem("p_exp")
    rd_done = sem("rd_done")
    p_done = sem("p_done")
    pt_done = sem("pt_done")
    pth_done = sem("pth_done")
    pt_read = sem("pt_read")
    pv_done = sem("pv_done")
    o_read = sem("o_read")
    y_done = sem("y_done")
    y_out = sem("y_out")
    x_in = [ctx.enter_context(nc.semaphore(f"x_in{k}")) for k in range(KT)]
    raw_in = (raw_in0, raw_in1, raw_in2)

    def lower(ap, h):
        return ap.rearrange("p (n two h) -> p n two h", two=2, h=h)[:, :, 0, :]

    def upper(ap, h):
        return ap.rearrange("p (n two h) -> p n two h", two=2, h=h)[:, :, 1, :]

    def seg(i):
        return slice(i * TU, (i + 1) * TU)

    def half(i):
        return slice(i * 512, (i + 1) * 512)

    def group_value(r, name):
        return r * NGROUP + GINDEX[name] + 1

    def read_value(r, name):
        who = GROUPS[GINDEX[name]][1]
        if who == "state":
            return st_step, NC * r + 4 * (int(name[1]) + 1)
        sem = read_act if who == "act" else read_dve
        return sem, (r + 1) * len(READS[who]) + READS[who].index(name) + 1

    def later(eng, sem, value):
        if type(value) is not int or value > 0:
            eng.wait_ge(sem, value)

    def bank(name):
        return R[GINDEX[name] % NBANK_R]

    def pt_count(q, kb):
        return 2 * q + kb + 1 - min(q, 3) - 1 if q < 4 else 2 * q + kb + 1 - 4

    block = ctx.enter_context(nc.Block())

    @block.sync
    def _(sp):
        def load_weights(n, slot, wait=True):
            if wait:
                sp.wait_ge(lo_done, n - 2)
            sp.dma_start(WR[:, slot], w_d[n]).then_inc(raw_in[slot], 16)

        for k in range(KT):
            sp.dma_start(A[:, k, :], x_d[:, k, :]).then_inc(x_in[k], 16)
            if k < 3:
                load_weights(k, k, wait=False)
            if k == 0:
                for t, d in ((ident[:], ident_d), (gain[:], gain_d), (lbw[:, 0], lbl_d),
                             (TA[:, 0:NL * P // 2], lmask_d)):
                    sp.dma_start(t, d).then_inc(const_in, 16)

        def states(r, first=False):
            if not first:
                sp.wait_ge(sts_out, 16 * r)
                sp.wait_ge(group_done, group_value(r - 1, "OS"))
            sp.dma_start(SS[:], st_d[r]).then_inc(ss_in, 16)

        def store_states(r):
            sp.wait_ge(st_step, NC * (r + 1))
            sp.dma_start(stp_d[r], ST[:, NC - 1, :]).then_inc(stp_out, 16)
            sp.wait_ge(ss_done, r + 1)
            sp.dma_start(sts_d[r], SS[:]).then_inc(sts_out, 16)

        states(0, first=True)
        for j in range(3):
            load_weights(3 + j, j)
        with sp.Fori(2, HEADS) as h:
            load_weights(3 * h, 0)
            load_weights(3 * h + 1, 1)
            store_states(h - 2)
            states(h - 1)
            load_weights(3 * h + 2, 2)
        for n in range(N_G, N_AO):
            load_weights(n, n % 3)
            if n == N_G + 1:
                store_states(HEADS - 2)
                states(HEADS - 1)
        store_states(HEADS - 1)
        def load_residual(use, src):
            if use >= 2:
                sp.wait_ge(unit_read, NU * (N_AO if use < KT else N_BO - KT) + NU * (use - 2) + 3)
            sp.dma_start(RES[use % 2][:], src).then_inc((res_in0, res_in1)[use % 2], 16)

        sp.wait_ge(stp_out, 16 * HEADS)
        sp.wait_ge(sts_out, 16 * HEADS)
        sp.wait_ge(g_done, HEADS)
        for t, d in ((amask, amask_d), (sink, sink_d), (smask, smask_d), (sinks, sinks_d), (CS, cs_d)):
            sp.dma_start(t[:], d).then_inc(const2_in, 16)
        for n in range(N_AO, N_AO + 3):
            load_weights(n, n % 3)
        for m in range(KT):
            load_residual(m, x_d[:, m, :])
            if m:
                sp.wait_ge(unit_read, NU * (N_AO + m))
                sp.dma_start(h1_d[:, m - 1, :], A[:, m - 1, :]).then_inc(h1_out, 16)
            load_weights(N_AO + m + 3, (N_AO + m + 3) % 3)
        sp.wait_ge(unit_read, NU * N_KV)
        sp.dma_start(h1_d[:, KT - 1, :], A[:, KT - 1, :]).then_inc(h1_out, 16)
        load_weights(N_BQ + 1, (N_BQ + 1) % 3)
        sp.wait_ge(k_rot, 1)
        sp.dma_start(kwin_d, EV[:, SEQ - P:T]).then_inc(k_out, 16)
        sp.wait_ge(v_raw, 1)
        sp.dma_start(vwin_d, RES[0][:, SEQ - P:T]).then_inc(v_out, 16)
        for n in range(N_BQ + 2, N_BG):
            load_weights(n, n % 3)
        sp.wait_ge(vn_done, 1)
        sp.wait_ge(v_out, 16)
        sp.dma_start(RES[0][:, 0:SEQ].rearrange("p (b w) -> p b w", b=DEC), kc_d).then_inc(cache_in, 16)
        sp.dma_start(RES[1][:, 0:SEQ].rearrange("p (b w) -> p b w", b=DEC), vc_d).then_inc(cache_in, 16)

        def store_gate(j):
            sp.wait_ge(gate_silu, j + 1)
            sp.dma_start(sg_d[:, j, :], EV2[:]).then_inc(sg_out, 16)

        for j in range(HP):
            load_weights(N_BG + j, (N_BG + j) % 3)
            if j >= 2:
                store_gate(j - 2)
        load_weights(N_BO, N_BO % 3)
        store_gate(HP - 2)
        load_weights(N_BO + 1, (N_BO + 1) % 3)
        store_gate(HP - 1)
        sp.wait_ge(sg_out, 16 * HP)
        for j in range(HP):
            if j >= 2:
                sp.wait_ge(gated, j - 1)
            else:
                sp.wait_ge(gate_silu, HP)
            sp.dma_start((EV, EV2)[j % 2][:], sg_d[:, j, :]).then_inc((sg_in0, sg_in1)[j % 2], 16)
        sp.wait_ge(h1_out, 16 * KT)
        sp.wait_ge(d_done, 1)
        for m in range(KT):
            if m >= 2:
                load_weights(N_BO + m, (N_BO + m) % 3)
            use = KT + m
            if m >= 2:
                sp.wait_ge(unit_read, NU * (N_BO + m - 2) + 3)
            sp.dma_start(RES[m % 2][:], h1_d[:, m, :]).then_inc((res_in0, res_in1)[m % 2], 16)
        for m in range(KT):
            sp.wait_ge(y_done, m + 1)
            sp.dma_start(y_d[:, m, :], A[:, m, :]).then_inc(y_out, 16)
        sp.wait_ge(k_out, 16)
        sp.wait_ge(y_out, 16 * KT)

    @block.gpsimd
    def _(pool):
        def gain_weights(n, slot, kind):
            uses = n // 3 if type(n) is int else None
            pool.wait_ge(raw_in[slot], 16 * (uses + 1) if uses is not None else 16 * (gain_weights.head + 1))
            nc.gpsimd.tensor_tensor(WR[:, slot], WR[:, slot], gain[:, kind, :].unsqueeze(2).broadcast_to([P, KT, P]),
                                    ALU.mult).then_inc(gained, 1)

        def difference(r, i, ref, blocks, width):
            nc.gpsimd.tensor_tensor(X[i % 3][:, 0:SEQ].rearrange("p (n w) -> p n w", w=width),
                                    B[:, 0:SEQ].rearrange("p (n w) -> p n w", w=width),
                                    B[:, ref:SEQ:width].unsqueeze(2).broadcast_to([P, blocks, width]),
                                    ALU.subtract).then_inc(dif_done, 1)

        def level(r, l):
            if l == 0:
                pool.wait_ge(b_scan, r + 1)
                later(pool, group_done, NGROUP * r)
            elif l < 3:
                later(pool, head_done, r)
            else:
                pool.wait_ge(group_done, group_value(r, f"L{LEVELS[l - 3]}"))
            h = LEVELS[l]
            difference(r, l, h - 1, SEQ // (2 * h), 2 * h)

        def recurrence(r, slot):
            if slot == 0:
                pool.wait_ge(b_log, r + 1)
                nc.gpsimd.tensor_tensor(K[:], B[:], RAWF[:], ALU.subtract).then_inc(k_log, 1)
            if slot == 1:
                pool.wait_ge(q_sig, r + 1)
                nc.gpsimd.tensor_tensor(Q[:], RAWQ[:], TA[:], ALU.mult).then_inc(q_done, 1)
                level(r, 0)
            if slot == 2:
                level(r, 1)
                level(r, 2)
            if slot == 3:
                level(r, 3)
                level(r, 4)
            if slot == 4:
                pool.wait_ge(qe_exp, r + 1)
                nc.gpsimd.tensor_tensor(QE[:].rearrange("p c w -> p (c w)"), QE[:].rearrange("p c w -> p (c w)"),
                                        Q[:, 0:SEQ], ALU.mult).then_inc(qe_done, 1)
                level(r, 5)
            if slot == 5:
                level(r, 6)
                pool.wait_ge(group_done, group_value(r, "L4"))
                difference(r, 7, P - 1, NC, P)
                pool.wait_ge(ss_in, 16 * (r + 1))
                pool.wait_ge(dec_done, r + 1)
                nc.gpsimd.tensor_tensor(SS[:], SS[:], DEC_C[:, NC:].unsqueeze(2).broadcast_to([P, DEC, P]),
                                        ALU.mult).then_inc(ss_decayed, 1)
            if slot == 6:
                pool.wait_ge(dif_exp, 8 * r + 8)
                nc.gpsimd.tensor_tensor(X[1][:, 0:SEQ], X[1][:, 0:SEQ], K[:, 0:SEQ], ALU.mult).then_inc(ke_done, 1)
            if slot == 7:
                pool.wait_ge(group_done, group_value(r, "L1"))
                pool.wait_ge(vs_done, r + 1)
                nc.gpsimd.tensor_tensor(X[0][:, 0:SEQ].rearrange("p (b e) -> p b e", b=DEC),
                                        ident[:].unsqueeze(1).broadcast_to([P, DEC, P]),
                                        VS[:].unsqueeze(2).broadcast_to([P, DEC, P]), ALU.mult).then_inc(vd_done, 1)

        pool.wait_ge(const_in, 16 * 4)
        for n in range(2):
            gain_weights(n, n, GAIN_A)

        def iteration(h, r):
            for slot in range(9):
                if slot % 3 == 0:
                    j = slot // 3
                    gain_weights.head = h if j == 0 else h + 1
                    gain_weights(3 * h + j + 2, (j + 2) % 3, GAIN_A)
                if r is not None:
                    recurrence(r, slot)

        iteration(0, None)
        iteration(1, 0)
        with pool.Fori(2, HEADS) as h:
            iteration(h, h - 1)
        for slot in range(9):
            if slot % 3 == 0:
                n = N_G + slot // 3 + 2
                gain_weights(n, n % 3, GAIN_A)
            recurrence(HEADS - 1, slot)

        def silu_gate(m):
            pool.wait_ge(g_sig, m + 1)
            nc.gpsimd.tensor_tensor(TA[:], TA[:], (RAWV, RAWF)[m % 2][:], ALU.mult).then_inc(g_silu, 1)

        silu_gate(0)
        silu_gate(1)
        for m in range(3, HEADS):
            if N_G + m + 2 < N_AO:
                gain_weights(N_G + m + 2, (N_G + m + 2) % 3, GAIN_A)
            silu_gate(m - 1)
        silu_gate(HEADS - 1)

        def gain_of(n):
            return GAIN_O if n < N_KV else GAIN_KV if n < N_BQ else GAIN_B

        def prepare(n):
            if n < N_BO:
                gain_weights(n, n % 3, gain_of(n))

        def add_square(m, base):
            pool.wait_ge(sq1_done, base + m + 1)
            if m == 0:
                ins = nc.gpsimd.tensor_copy(SQA[:], SQ[:])
            else:
                pool.wait_ge(sq1_added, base + m)
                ins = nc.gpsimd.tensor_tensor(SQA[:], SQA[:], SQ[:], ALU.add)
            ins.then_inc(sq1_added, 1)

        prepare(N_AO)
        prepare(N_AO + 1)
        for m in range(KT):
            prepare(N_AO + m + 2)
            add_square(m, 0)
        for n in range(N_KV + 2, N_KV + 4):
            prepare(n)
        for j in range(HP):
            prepare(N_BQ + j + 2)
            pool.wait_ge(q_raw, j + 1)
            pool.wait_ge(q_shuffled, j + 1)
            nc.gpsimd.tensor_tensor(EV[:], EV[:], CS[:, 0], ALU.mult).then_inc(q_cos, 1)
        for j in range(HP):
            prepare(N_BG + j + 2)
            for p in range(4):
                q = 4 * j + p
                pool.wait_ge(rd_done, q + 1)
                keys = slice(P if j == 0 else 0, 2 * P)
                sp_ = SP_[q % 2][:, :, keys]
                nc.gpsimd.tensor_tensor(sp_, sp_, small[:, q % 2, 5, :].unsqueeze(2).broadcast_to(
                    [P, 4, keys.stop - keys.start]), ALU.mult).then_inc(p_done, 1)
                if p == 2:
                    pool.wait_ge(gate_sig, j + 1)
                    nc.gpsimd.tensor_tensor(EV2[:], EV2[:], EV[:], ALU.mult).then_inc(gate_silu, 1)
        for m in range(KT):
            add_square(m, KT)

    @block.scalar
    def _(act):
        nc.scalar.preload_act_table_set("natural_log_exp_and_others")

        def high_part(n, slot, first=False):
            act.wait_ge(gained, n + 1)
            if not first:
                act.wait_ge(unit_done, NU * n - 6)
            nc.scalar.activation(WH[:, slot], WR[:, slot], ACT.Copy).then_inc(hi_done, 1)

        def exp_halves(r, l):
            h = LEVELS[l]
            x = X[l % 3][:, 0:SEQ]
            act.wait_ge(dif_done, 8 * r + l + 1)
            nc.scalar.activation(lower(x, h), lower(x, h), ACT.Exp, scale=-1.0)
            nc.scalar.activation(upper(x, h), upper(x, h), ACT.Exp).then_inc(dif_exp, 1)

        NLINK = 5

        def recurrence(r, slot):
            link = [0]

            def chained(ins, r=r):
                link[0] += 1
                ins.then_inc(act_link, 1)
                act.wait_ge(act_link, NLINK * r + link[0])

            if slot == 0:
                act.wait_ge(unit_read, 9 * r + 6)
                later(act, q_done, r)
                act.wait_ge(masks_done, 1)
                chained(nc.scalar.activation(TA[:], RAWF[:], ACT.Abs))
                chained(nc.scalar.activation(TA[:], TA[:], ACT.Exp, scale=-1.0))
                nc.scalar.activation(TA[:], TA[:], ACT.Ln, bias=1.0).then_inc(f_soft, 1)
                for i in range(2):
                    act.wait_ge(group_done, group_value(r, f"VT{i}"))
                    nc.scalar.activation(VH[:, 4 * i:4 * i + 4].rearrange("p c w -> p (c w)"), bank(f"VT{i}")[:],
                                         ACT.Copy).then_inc(read_act, 1)
                act.wait_ge(k_log, r + 1)
                nc.scalar.activation(K[:], K[:], ACT.Exp).then_inc(k_exp, 1)
                chained(nc.scalar.activation(TA[:], RAWF[:], ACT.Exp, scale=-1.0))
                act.wait_ge(head_lb, r + 1)
                nc.scalar.activation(TA[:], TA[:], ACT.Ln, scale=lbh[:, 0:1], bias=1.0).then_inc(lb_ln, 1)
            link[0] = 3
            if slot == 1:
                act.wait_ge(unit_read, 9 * r + 9)
                act.wait_ge(b_add, r + 1)
                chained(nc.scalar.activation(TA[:], RAWQ[:], ACT.Abs))
                chained(nc.scalar.activation(TA[:], TA[:], ACT.Exp, scale=-1.0))
                nc.scalar.activation(TA[:], TA[:], ACT.Ln, bias=1.0).then_inc(q_soft, 1)
                act.wait_ge(q_log, r + 1)
                nc.scalar.activation(TA[:], Q[:], ACT.Exp).then_inc(q_sig, 1)
                act.wait_ge(b_scan, r + 1)
                nc.scalar.activation(DEC_C[:, 0:NC], B[:, P - 1:SEQ:P], ACT.Exp)
                nc.scalar.activation(DEC_C[:, NC:], B[:, SEQ:T], ACT.Exp).then_inc(dec_done, 1)
                exp_halves(r, 0)
            if slot == 2:
                exp_halves(r, 1)
                exp_halves(r, 2)
            if slot == 3:
                exp_halves(r, 3)
                nc.scalar.activation(QE[:].rearrange("p c w -> p (c w)"), B[:, 0:SEQ], ACT.Exp).then_inc(qe_exp, 1)
                exp_halves(r, 4)
            if slot == 4:
                exp_halves(r, 5)
            if slot == 5:
                exp_halves(r, 6)
                act.wait_ge(dif_done, 8 * r + 8)
                nc.scalar.activation(X[1][:, 0:SEQ], X[1][:, 0:SEQ], ACT.Exp, scale=-1.0).then_inc(dif_exp, 1)
            if slot == 7:
                for i in range(2):
                    act.wait_ge(group_done, group_value(r, f"T{i}"))
                    nc.scalar.activation(X[2][:, half(i)], bank(f"T{i}")[:], ACT.Copy).then_inc(read_act, 1)
            if slot == 8:
                sem, value = read_value(r, "OS")
                act.wait_ge(sem, value)
                nc.scalar.activation(X[0][:], X[2][:], ACT.Square).then_inc(osq_done, 1)
                for i in range(NU):
                    act.wait_ge(group_done, group_value(r, f"N{i}"))
                    nc.scalar.activation(X[1][:, seg(i)], bank(f"N{i}")[:, 0:TU], ACT.Ln, scale=1.0 / P, bias=eps[:]
                                         ).then_inc(read_act, 1)
                sem, value = read_value(r, "N2")
                act.wait_ge(sem, value)
                nc.scalar.activation(X[1][:], X[1][:], ACT.Exp, scale=-0.5).then_inc(rn_done, 1)

        act.wait_ge(lbl_diff, 1)
        nc.scalar.activation(lbw[:, 1], lbw[:, 1], ACT.Exp).then_inc(lbl_exp, 1)
        for k in range(KT):
            act.wait_ge(x_in[k], 16)
            if k >= 3:
                act.wait_ge(sq_used, k - 2)
            nc.scalar.activation(X[k % 3][:], A[:, k, :], ACT.Square).then_inc(sq_done, 1)
        act.wait_ge(setup_dve, 1)
        for n in range(2):
            high_part(n, n, first=True)
        act.wait_ge(sq_used, KT)
        for i in range(NU):
            ins = nc.scalar.activation(RB[:, seg(i)], R[i][:, 0:TU], ACT.Ln, scale=1.0 / D, bias=eps[:])
        ins.then_inc(ln_done, 1)
        act.wait_ge(ln_done, 1)
        nc.scalar.activation(RB[:], RB[:], ACT.Exp, scale=-0.5).then_inc(rb_done, 1)
        act.wait_ge(rb_done, 1)
        nc.scalar.activation(spare[:, 0:1], RB[:, 0:1], ACT.Copy).then_inc(read_act, len(READS["act"]))

        def iteration(h, r):
            for slot in range(9):
                if slot % 3 == 0:
                    j = slot // 3
                    high_part(3 * h + j + 2, (j + 2) % 3, first=(type(h) is int and h == 0 and j == 0))
                if r is not None:
                    recurrence(r, slot)

        iteration(0, None)
        iteration(1, 0)
        with act.Fori(2, HEADS) as h:
            iteration(h, h - 1)
        for slot in range(9):
            if slot % 3 == 0:
                n = N_G + slot // 3 + 2
                high_part(n, n % 3)
            recurrence(HEADS - 1, slot)

        link = [NLINK * HEADS]

        def chained(ins):
            link[0] += 1
            ins.then_inc(act_link, 1)
            act.wait_ge(act_link, link[0])

        def silu_gate(m):
            raw = (RAWV, RAWF)[m % 2]
            act.wait_ge(unit_read, NU * (N_G + m) + 3)
            if m:
                act.wait_ge(g_done, m)
            chained(nc.scalar.activation(TA[:], raw[:], ACT.Abs))
            chained(nc.scalar.activation(TA[:], TA[:], ACT.Exp, scale=-1.0))
            nc.scalar.activation(TA[:], TA[:], ACT.Ln, bias=1.0).then_inc(g_soft, 1)
            act.wait_ge(g_log, m + 1)
            nc.scalar.activation(TA[:], TA[:], ACT.Exp).then_inc(g_sig, 1)

        silu_gate(0)
        silu_gate(1)
        for m in range(3, HEADS):
            if N_G + m + 2 < N_AO:
                high_part(N_G + m + 2, (N_G + m + 2) % 3)
            silu_gate(m - 1)
        silu_gate(HEADS - 1)

        def prepare(n):
            if n >= NBLK:
                return
            if n < N_BO:
                high_part(n, n % 3)
            else:
                act.wait_ge(raw_in[n % 3], 16 * (n // 3 + 1))
                act.wait_ge(unit_done, NU * n - 6)
                nc.scalar.activation(WH[:, n % 3], WR[:, n % 3], ACT.Copy).then_inc(hi_done, 1)

        def cut(k, stage):
            nc.scalar.activation(XH[:, k, :], A[:, k, :], ACT.Copy).then_inc(cut_hi, 1)

        def square(m, n, base):
            act.wait_ge(unit_read, NU * n + 3)
            if base + m:
                act.wait_ge(sq1_added, base + m)
            nc.scalar.activation(SQ[:], A[:, m, :], ACT.Square).then_inc(sq1_done, 1)

        def rms(turn):
            act.wait_ge(sums1_done, turn)
            for i in range(NU):
                ins = nc.scalar.activation(RB[:, seg(i)], R[i][:, 0:TU], ACT.Ln, scale=1.0 / D, bias=eps[:])
            ins.then_inc(ln1_done, 1)
            act.wait_ge(ln1_done, turn)
            nc.scalar.activation(RB[:], RB[:], ACT.Exp, scale=-0.5).then_inc(rb1_done, 1)

        prepare(N_AO)
        prepare(N_AO + 1)
        act.wait_ge(unit_done, NU * N_AO)
        for k in range(KT):
            act.wait_ge(g_done, k + 1)
            cut(k, 0)
        for m in range(KT):
            prepare(N_AO + m + 2)
            square(m, N_AO + m, 0)
        act.wait_ge(unit_done, NU * N_KV)
        for k in range(KT):
            cut(k, 1)
        rms(1)
        prepare(N_KV + 2)
        act.wait_ge(k_rot, 1)
        act.wait_ge(kb_zero, 1)
        nc.scalar.activation(KBH[0:64, 0, :], EV[0:64, 0:SEQ], ACT.Copy)
        nc.scalar.activation(KBH[64:P, 1, :], EV[64:P, 0:SEQ], ACT.Copy).then_inc(kb_high, 1)
        prepare(N_KV + 3)
        for i in range(2):
            act.wait_ge(v_turned, i + 1)
            nc.scalar.activation(VPH[:, 4 * i:4 * i + 4].rearrange("p c (z w) -> p c z w", z=3)[:, :, 0:3:2, :],
                                 R[3 + i][:].rearrange("p (c v w) -> p c v w", c=4, v=2), ACT.Copy
                                 ).then_inc(vp_high, 1)
        for j in range(HP):
            prepare(N_BQ + j + 2)

        act.wait_ge(d_max, 1)
        nc.scalar.activation(SSN[:], SSN[:], ACT.Exp, bias=dsm[:, 1:2], accum_out=dsm[:, 3:4])
        nc.scalar.activation(dsm[:, 4:5], dsm[:, 2:3], ACT.Exp).then_inc(d_exp, 1)

        def cut_queries(nb):
            if nb:
                act.wait_ge(sc_done, 8 * nb)
            nc.scalar.activation(QNH[:], A[:, :, nb * P:(nb + 1) * P], ACT.Copy).then_inc(qn_high, 1)

        def exponentials(q):
            keys = slice(P if q < 4 else 0, 2 * P)
            act.wait_ge(m_ready, q + 1)
            sm = small[:, q % 2]
            for i in range(4):
                nc.scalar.activation(SP_[q % 2][:, i, keys], SP_[q % 2][:, i, keys], ACT.Exp, bias=sm[:, 1, i:i + 1],
                                     accum_out=sm[:, 3, i:i + 1])
            nc.scalar.activation(sm[:, 4, :], sm[:, 2, :], ACT.Exp).then_inc(p_exp, 1)

        def turned_high(q):
            for kb in range(1 if q < 4 else 0, 2):
                act.wait_ge(pt_done, pt_count(q, kb))
                if q:
                    act.wait_ge(pv_done, q)
                nc.scalar.activation(PTH[:, kb, :], R[2 + kb][:], ACT.Copy).then_inc(pth_done, 1)

        def take_output(q):
            nb, p = divmod(q, 4)
            act.wait_ge(pv_done, q + 1)
            nc.scalar.activation(A[:, 2 * p:2 * p + 2, nb * P:(nb + 1) * P],
                                 R[4][:, 0:2 * P].rearrange("p (j w) -> p j w", j=2), ACT.Copy).then_inc(o_read, 1)

        glink = [NLINK * HEADS + 2 * HEADS]
        act.wait_ge(d_done, 1)
        cut_queries(0)
        for q in range(32):
            j, p = divmod(q, 4)
            exponentials(q)
            if q:
                turned_high(q - 1)
                take_output(q - 1)
            if p == 0:
                prepare(N_BG + j + 2)
            if p == 1:
                act.wait_ge(unit_read, NU * (N_BG + j) + 3)
                if j:
                    act.wait_ge(sg_out, 16 * j)
                for ins in (nc.scalar.activation(EV2[:], EV[:], ACT.Abs),):
                    glink[0] += 1
                    ins.then_inc(act_link, 1)
                    act.wait_ge(act_link, glink[0])
                glink[0] += 1
                nc.scalar.activation(EV2[:], EV2[:], ACT.Exp, scale=-1.0).then_inc(act_link, 1)
                act.wait_ge(act_link, glink[0])
                nc.scalar.activation(EV2[:], EV2[:], ACT.Ln, bias=1.0).then_inc(gate_soft, 1)
            if p == 2:
                act.wait_ge(gate_log, j + 1)
                nc.scalar.activation(EV2[:], EV2[:], ACT.Exp).then_inc(gate_sig, 1)
            if p == 2 and j < HP - 1:
                pass
            if p == 3 and j < HP - 1:
                cut_queries(j + 1)
        turned_high(31)
        take_output(31)
        act.wait_ge(unit_done, NU * N_BO)
        for k in range(KT):
            act.wait_ge(gated, k + 1)
            cut(k, 2)
        for m in range(KT):
            prepare(N_BO + m + 2)
            square(m, N_BO + m, KT)
        rms(2)

    @block.vector
    def _(dve):
        def rest_part(n, slot):
            dve.wait_ge(hi_done, n + 1)
            nc.vector.tensor_tensor(WL[:, slot], WR[:, slot], WH[:, slot].bitcast(fp32), ALU.subtract
                                    ).then_inc(lo_done, 1)

        def evacuate(u, i, dst):
            dve.wait_ge(unit_done, u + 1)
            nc.vector.tensor_tensor(dst[:, seg(i)], G[i][:, 0:TU], RB[:, seg(i)], ALU.mult).then_inc(unit_read, 1)

        def merge(r, name, out, mask, data):
            dve.wait_ge(group_done, group_value(r, name))
            sem, value = read_value(r, name)
            dve.wait_ge(sem, value - 1)
            nc.vector.memset(tick[:], 0.0)
            nc.vector.copy_predicated(out, mask, data).then_inc(read_dve, 1)

        def merge_diagonal(r, i):
            merge(r, f"D{i}", AT[:, 4 * i:4 * i + 4], imask[:].unsqueeze(1).broadcast_to([P, 4, P]),
                  bank(f"D{i}")[:].rearrange("p (c w) -> p c w", c=4))

        def merge_level(r, l):
            h = LEVELS[l]
            nb = P // (2 * h)
            merge(r, f"L{h}", AT[:].rearrange("p c (n two h) -> p c n two h", two=2, h=h)[:, :, :, 1, :],
                  lmask[:, l, :].rearrange("p (n h) -> p n h", h=h).unsqueeze(1).broadcast_to([P, NC, nb, h]),
                  bank(f"L{h}")[:].rearrange("p (c n h) -> p c n h", c=NC, h=h))

        def decayed(r, l):
            h = LEVELS[l]
            x = X[l % 3][:, 0:SEQ]
            dve.wait_ge(dif_exp, 8 * r + l + 1)
            nc.vector.tensor_tensor(lower(x, h), lower(x, h), lower(K[:, 0:SEQ], h), ALU.mult)
            nc.vector.tensor_tensor(upper(x, h), upper(x, h), upper(Q[:, 0:SEQ], h), ALU.mult
                                    ).then_inc(level_done, 1)

        def recurrence_make(r, slot):
            if slot == 0:
                later(dve, lb_ln, r)
                nc.vector.tensor_copy(lbh[:], lb2[:, r, :]).then_inc(head_lb, 1)
                dve.wait_ge(unit_read, 9 * r + 3)
                later(dve, vd_done, r)
                nc.vector.tensor_copy(VS[:], RAWV[:, SEQ:T]).then_inc(vs_done, 1)
                dve.wait_ge(f_soft, r + 1)
                dve.wait_ge(unit_read, 9 * r + 6)
                nc.vector.scalar_tensor_tensor(B[:], RAWF[:], 0.0, TA[:], ALU.min, ALU.subtract).then_inc(b_log, 1)
                dve.wait_ge(k_exp, r + 1)
                dve.wait_ge(head_lb, r + 1)
                nc.vector.tensor_scalar(K[:], K[:], lbh[:, 1:2], None, ALU.mult).then_inc(k_done, 1)
                dve.wait_ge(lb_ln, r + 1)
                dve.wait_ge(b_log, r + 1)
                nc.vector.tensor_tensor(B[:], B[:], TA[:], ALU.add).then_inc(b_add, 1)
                dve.wait_ge(b_add, r + 1)
                nc.vector.tensor_tensor_scan(B[:], carry[:], B[:], 0.0, ALU.mult, ALU.add).then_inc(b_scan, 1)
            if slot == 1:
                dve.wait_ge(q_soft, r + 1)
                dve.wait_ge(unit_read, 9 * r + 9)
                nc.vector.scalar_tensor_tensor(Q[:], RAWQ[:], 0.0, TA[:], ALU.min, ALU.subtract).then_inc(q_log, 1)
            if slot == 2:
                dve.wait_ge(k_done, r + 1)
                dve.wait_ge(q_done, r + 1)
                decayed(r, 0)
                decayed(r, 1)
            if slot == 3:
                decayed(r, 2)
            if slot == 4:
                decayed(r, 3)
                decayed(r, 4)
            if slot == 5:
                decayed(r, 5)
            if slot == 6:
                decayed(r, 6)

        def recurrence_read(r, slot):
            if slot == 2:
                merge_diagonal(r, 0)
                merge_diagonal(r, 1)
                merge_level(r, 0)
            if slot == 3:
                merge_level(r, 1)
                merge_level(r, 2)
            if slot == 4:
                merge_level(r, 3)
            if slot == 5:
                merge_level(r, 4)
                merge_level(r, 5)
            if slot == 6:
                merge_level(r, 6)
            if slot == 8:
                for i in range(2):
                    dve.wait_ge(group_done, group_value(r, f"VB{i}"))
                    nc.vector.tensor_tensor(X[1][:, half(i)].rearrange("p (b e) -> p b e", b=4),
                                            bank(f"VB{i}")[:].rearrange("p (b e) -> p b e", b=4),
                                            K[:, SEQ + 4 * i:SEQ + 4 * i + 4].unsqueeze(2).broadcast_to([P, 4, P]),
                                            ALU.mult).then_inc(read_dve, 1)
                dve.wait_ge(*read_value(r, "VB1"))
                dve.wait_ge(ss_decayed, r + 1)
                nc.vector.tensor_tensor(SS[:], SS[:], X[1][:, 0:SEQ].rearrange("p (b e) -> p b e", b=DEC), ALU.add
                                        ).then_inc(ss_done, 1)
                later(dve, stp_out, 16 * r)
                for c in range(NC):
                    ps = bank(f"S{c // 4}")[:, (c % 4) * P:(c % 4 + 1) * P]
                    if c % 4 == 0:
                        dve.wait_ge(group_done, group_value(r, f"S{c // 4}"))
                    if c == 0:
                        ins = nc.vector.tensor_copy(ST[:, 0, :], ps)
                    else:
                        dve.wait_ge(st_step, NC * r + c)
                        ins = nc.vector.scalar_tensor_tensor(ST[:, c, :], ST[:, c - 1, :], DEC_C[:, c:c + 1], ps,
                                                             ALU.mult, ALU.add)
                    ins.then_inc(st_step, 1)

        def finish_head(r):
            for name, cols in (("O0", half(0)), ("O1", half(1)), ("OS", slice(SEQ, T))):
                dve.wait_ge(group_done, group_value(r, name))
                nc.vector.tensor_copy(X[2][:, cols], bank(name)[:, 0:cols.stop - cols.start]).then_inc(read_dve, 1)
            dve.wait_ge(rn_done, r + 1)
            nc.vector.tensor_tensor(A[:, r, :], X[2][:], X[1][:], ALU.mult).then_inc(head_done, 1)

        nc.vector.memset(ones[:], 1.0)
        nc.vector.memset(eps[:], EPS).then_inc(setup_dve, 1)
        nc.vector.memset(carry[:], 1.0).then_inc(setup_dve, 1)
        dve.wait_ge(setup_dve, 2)
        nc.vector.memset(carry[:, 0:SEQ:P], 0.0)
        nc.vector.memset(carry[:, SEQ:T], 0.0).then_inc(setup_dve, 1)
        dve.wait_ge(setup_dve, 3)
        nc.vector.memset(AT[:], 0.0).then_inc(read_dve, len(READS["dve"]))
        dve.wait_ge(const_in, 16 * 4)
        nc.vector.tensor_tensor(lbw[:, 1], lbw[:, 0], lbw[:, 0], ALU.subtract).then_inc(lbl_diff, 1)
        nc.vector.tensor_copy(imask[:], ident[:])
        nc.vector.tensor_copy(lmask[:].rearrange("p l w -> p (l w)"), TA[:, 0:NL * P // 2]).then_inc(masks_done, 1)
        dve.wait_ge(lbl_exp, 1)
        nc.vector.reciprocal(lbw[:, 2], lbw[:, 1]).then_inc(lb_done, 1)
        dve.wait_ge(lb_done, 1)
        nc.vector.tensor_tensor(lbw[:, 3], lbw[:, 1], lbw[:, 2], ALU.mult).then_inc(lb_done, 1)
        dve.wait_ge(lb_done, 2)
        nc.vector.tensor_tensor(lb2[:, :, 0], lbw[:, 3], lbw[:, 3], ALU.subtract).then_inc(lb_done, 1)
        dve.wait_ge(lb_done, 3)
        nc.vector.tensor_scalar(lb2[:, :, 1], lb2[:, :, 0], -1.0, 1.0, ALU.mult, ALU.add).then_inc(lb_done, 1)
        dve.wait_ge(lb_done, 4)
        for n in range(2):
            rest_part(n, n)
        for k in range(KT):
            dve.wait_ge(x_in[k], 16)
            nc.vector.tensor_copy(XH[:, k, :], A[:, k, :]).then_inc(x_split, 1)
            dve.wait_ge(x_split, 2 * k + 1)
            nc.vector.tensor_tensor(XL[:, k, :], A[:, k, :], XH[:, k, :].bitcast(fp32), ALU.subtract
                                    ).then_inc(x_split, 1)
        dve.wait_ge(rb_done, 1)
        dve.wait_ge(masks_done, 1)

        def iteration(h, r):
            for slot in range(9):
                j, i = divmod(slot, 3)
                if i == 0:
                    rest_part(3 * h + j + 2, (j + 2) % 3)
                if r is not None:
                    recurrence_make(r, slot)
                evacuate(9 * h + slot, i, (RAWV, RAWF, RAWQ)[j])
                if r is not None:
                    recurrence_read(r, slot)
            if r is not None:
                finish_head(r)

        iteration(0, None)
        iteration(1, 0)
        with dve.Fori(2, HEADS) as h:
            iteration(h, h - 1)

        def gate_raw(m):
            return (RAWV, RAWF)[m % 2]

        def silu_gate_log(m):
            dve.wait_ge(g_soft, m + 1)
            nc.vector.scalar_tensor_tensor(TA[:], gate_raw(m)[:], 0.0, TA[:], ALU.min, ALU.subtract
                                           ).then_inc(g_log, 1)

        def silu_gate_apply(m):
            dve.wait_ge(g_silu, m + 1)
            nc.vector.tensor_tensor(A[:, m, :], A[:, m, :], TA[:], ALU.mult).then_inc(g_done, 1)

        for slot in range(9):
            m, i = divmod(slot, 3)
            if i == 0:
                rest_part(N_G + m + 2, (N_G + m + 2) % 3)
            recurrence_make(HEADS - 1, slot)
            if m < 2:
                evacuate(NU * (N_G + m) + i, i, gate_raw(m))
            recurrence_read(HEADS - 1, slot)
        finish_head(HEADS - 1)
        dve.wait_ge(head_done, HEADS)
        silu_gate_log(0)
        silu_gate_apply(0)
        for i in range(NU):
            evacuate(NU * (N_G + 2) + i, i, gate_raw(2))
        silu_gate_log(1)
        silu_gate_apply(1)
        for m in range(3, HEADS):
            if N_G + m + 2 < N_AO:
                rest_part(N_G + m + 2, (N_G + m + 2) % 3)
            for i in range(NU):
                evacuate(NU * (N_G + m) + i, i, gate_raw(m))
            silu_gate_log(m - 1)
            silu_gate_apply(m - 1)
        silu_gate_log(HEADS - 1)
        silu_gate_apply(HEADS - 1)

        small_link = [0]

        def chained(ins):
            small_link[0] += 1
            ins.then_inc(dve_small, 1)
            dve.wait_ge(dve_small, small_link[0])

        def prepare(n):
            if n < NBLK:
                rest_part(n, n % 3)

        def cut(k, stage):
            dve.wait_ge(cut_hi, KT * stage + k + 1)
            nc.vector.tensor_tensor(XL[:, k, :], A[:, k, :], XH[:, k, :].bitcast(fp32), ALU.subtract
                                    ).then_inc(cut_lo, 1)

        def add_residual(n, m, use):
            for i in range(NU):
                dve.wait_ge(unit_done, NU * n + i + 1)
                dve.wait_ge((res_in0, res_in1)[m % 2], 16 * (use // 2 + 1))
                nc.vector.tensor_tensor(A[:, m, seg(i)], G[i][:, 0:TU], RES[m % 2][:, seg(i)], ALU.add
                                        ).then_inc(unit_read, 1)

        SWAP = [*range(8, 16), *range(0, 8), *range(16, 32)]

        def rotate_swap():
            nc.vector.stream_shuffle(EV2[:], EV[:], SWAP).then_inc(q_shuffled, 1)

        prepare(N_AO)
        prepare(N_AO + 1)
        for k in range(KT):
            cut(k, 0)
        for m in range(KT):
            prepare(N_AO + m + 2)
            add_residual(N_AO + m, m, m)
        for k in range(KT):
            cut(k, 1)
        dve.wait_ge(rb1_done, 1)
        for i in range(NU):
            evacuate(NU * N_KV + i, i, EV)
        dve.wait_ge(unit_read, NU * N_KV + 3)
        dve.wait_ge(const2_in, 16 * 5)
        chained(nc.vector.stream_shuffle(EV2[:], EV[:], SWAP))
        nc.vector.tensor_tensor(EV[:], EV[:], CS[:, 0], ALU.mult)
        chained(nc.vector.tensor_tensor(EV2[:], EV2[:], CS[:, 1], ALU.mult))
        nc.vector.tensor_tensor(EV[:], EV[:], EV2[:], ALU.add).then_inc(k_rot, 1)
        nc.vector.memset(KBH[64:P, 0, :].bitcast(fp32), 0.0)
        nc.vector.memset(KBH[0:64, 1, :].bitcast(fp32), 0.0)
        nc.vector.memset(KBL[64:P, 0, :].bitcast(fp32), 0.0)
        nc.vector.memset(KBL[0:64, 1, :].bitcast(fp32), 0.0)
        for t in (VPH, VPL):
            ins = nc.vector.memset(t[:, :, 64:128].bitcast(fp32), 0.0)
        ins.then_inc(kb_zero, 1)
        for i in range(NU):
            evacuate(NU * (N_KV + 1) + i, i, RES[0])
        dve.wait_ge(unit_read, NU * N_BQ)
        nc.vector.tensor_copy(dsm[:, 5:6], RES[0][:, 0:1]).then_inc(v_raw, 1)
        prepare(N_KV + 2)
        dve.wait_ge(k_rot, 1)
        nc.vector.tensor_copy(KSN[:], EV[:, SEQ:T])
        dve.wait_ge(kb_high, 1)
        nc.vector.tensor_tensor(KBL[0:64, 0, :], EV[0:64, 0:SEQ], KBH[0:64, 0, :].bitcast(fp32), ALU.subtract)
        nc.vector.tensor_tensor(KBL[64:P, 1, :], EV[64:P, 0:SEQ], KBH[64:P, 1, :].bitcast(fp32), ALU.subtract
                                ).then_inc(kb_done, 1)
        prepare(N_KV + 3)
        for i in range(2):
            dve.wait_ge(vp_high, i + 1)
            view = [t[:, 4 * i:4 * i + 4].rearrange("p c (z w) -> p c z w", z=3)[:, :, 0:3:2, :] for t in (VPH, VPL)]
            nc.vector.tensor_tensor(view[1], R[3 + i][:].rearrange("p (c v w) -> p c v w", c=4, v=2),
                                    view[0].bitcast(fp32), ALU.subtract).then_inc(vp_done, 1)
        dve.wait_ge(v_turned, 3)
        nc.vector.tensor_copy(VN[:], R[2][0:DEC, 0:P]).then_inc(vn_done, 1)
        dve.wait_ge(k_out, 16)
        dve.wait_ge(kb_done, 1)
        dve.wait_ge(h1_out, 16 * KT)
        for j in range(HP):
            prepare(N_BQ + j + 2)
            for i in range(NU):
                u = NU * (N_BQ + j) + i
                dve.wait_ge(unit_done, u + 1)
                if j:
                    dve.wait_ge(q_rot, j)
                nc.vector.scalar_tensor_tensor(EV[:, seg(i)], G[i][:, 0:TU], 0.125, RB[:, seg(i)], ALU.mult, ALU.mult
                                               ).then_inc(unit_read, 1)
            dve.wait_ge(unit_read, NU * (N_BQ + j) + 3)
            nc.vector.tensor_copy(dsm[:, 5:6], EV[:, 0:1]).then_inc(q_raw, 1)
            rotate_swap()
            dve.wait_ge(q_shuffled, j + 1)
            nc.vector.tensor_tensor(EV2[:], EV2[:], CS[:, 1], ALU.mult).then_inc(q_sin, 1)
            dve.wait_ge(q_cos, j + 1)
            dve.wait_ge(q_sin, j + 1)
            nc.vector.tensor_tensor(A[:, j, :], EV[:], EV2[:], ALU.add).then_inc(q_rot, 1)
        dve.wait_ge(q_rot, HP)
        chained(nc.vector.memset(QS[:], 0.0))
        nc.vector.tensor_copy(QS[0:64, :, 0, :], A[0:64, :, SEQ:T].rearrange("p j b -> p b j"))
        nc.vector.tensor_copy(QS[64:P, :, 1, :], A[64:P, :, SEQ:T].rearrange("p j b -> p b j")).then_inc(d_qs, 1)
        evacuate(NU * N_BG, 0, EV)
        dve.wait_ge(d_scores, 1)
        nc.vector.tensor_copy(SST[:], R[0][:, 0:P])
        nc.vector.tensor_tensor(SSN[:, P:], R[1][:, 0:DEC], smask[:], ALU.add).then_inc(d_copied, 1)
        evacuate(NU * N_BG + 1, 1, EV)
        dve.wait_ge(d_turned, 1)
        chained(nc.vector.tensor_copy(SSN[:, 0:P], R[2][:, 0:P]))
        chained(nc.vector.reduce_max(dsm[:, 0:1], SSN[:], AX.X))
        chained(nc.vector.tensor_tensor(dsm[:, 0:1], dsm[:, 0:1], sinks[:], ALU.max))
        chained(nc.vector.tensor_scalar(dsm[:, 1:2], dsm[:, 0:1], -1.0, None, ALU.mult))
        nc.vector.tensor_tensor(dsm[:, 2:3], dsm[:, 1:2], sinks[:], ALU.add).then_inc(d_max, 1)
        dve.wait_ge(d_exp, 1)
        chained(nc.vector.tensor_tensor(dsm[:, 3:4], dsm[:, 3:4], dsm[:, 4:5], ALU.add))
        chained(nc.vector.reciprocal(dsm[:, 4:5], dsm[:, 3:4]))
        nc.vector.tensor_scalar(SSN[:], SSN[:], dsm[:, 4:5], None, ALU.mult).then_inc(d_prob, 1)
        evacuate(NU * N_BG + 2, 2, EV)
        dve.wait_ge(d_ptur, 1)
        nc.vector.tensor_copy(PST[:], R[3][:, 0:P])
        nc.vector.tensor_copy(PSN[:], R[4][0:DEC, 0:P]).then_inc(d_pcop, 1)
        dve.wait_ge(d_out, 1)
        res = R[0][:, 0:P].rearrange("p (b v j) -> p b v j", b=DEC, v=2)
        nc.vector.tensor_copy(A[0:64, :, SEQ:T].rearrange("p j b -> p b j"), res[0:64, :, 0, :])
        nc.vector.tensor_copy(A[64:P, :, SEQ:T].rearrange("p j b -> p b j"), res[64:P, :, 1, :]).then_inc(d_done, 1)

        def cut_queries(nb):
            dve.wait_ge(qn_high, nb + 1)
            if nb:
                dve.wait_ge(sc_done, 8 * nb)
            nc.vector.tensor_tensor(QNL[:], A[:, :, nb * P:(nb + 1) * P], QNH[:].bitcast(fp32), ALU.subtract
                                    ).then_inc(qn_done, 1)

        def maxima(q):
            keys = slice(P if q < 4 else 0, 2 * P)
            sm = small[:, q % 2]
            if q >= 2:
                dve.wait_ge(pt_done, pt_count(q - 2, 1))
            for jj in range(2):
                dve.wait_ge(sc_done, 2 * q + jj + 1)
                ps = R[jj][:].rearrange("p (v w) -> p v w", v=2)
                for v in range(2):
                    i = 2 * jj + v
                    h = 4 * (q % 4) + i
                    ins = nc.vector.tensor_tensor_reduce(
                        out=SP_[q % 2][:, i, keys], in0=ps[:, v, keys], in1=amask[:, keys], scale=1.0,
                        scalar=sink[:, h:h + 1], op0=ALU.add, op1=ALU.max, accum_out=sm[:, 0, i:i + 1])
                ins.then_inc(sc_read, 1)
            dve.wait_ge(sc_read, 2 * q + 2)
            chained(nc.vector.tensor_scalar(sm[:, 1, :], sm[:, 0, :], -1.0, None, ALU.mult))
            nc.vector.tensor_tensor(sm[:, 2, :], sm[:, 1, :], sink[:, 4 * (q % 4):4 * (q % 4) + 4], ALU.add
                                    ).then_inc(m_ready, 1)

        def denominators(q):
            sm = small[:, q % 2]
            dve.wait_ge(p_exp, q + 1)
            chained(nc.vector.tensor_tensor(sm[:, 3, :], sm[:, 3, :], sm[:, 4, :], ALU.add))
            nc.vector.reciprocal(sm[:, 5, :], sm[:, 3, :]).then_inc(rd_done, 1)

        def turned_rest(q):
            for kb in range(1 if q < 4 else 0, 2):
                dve.wait_ge(pth_done, pt_count(q, kb))
                nc.vector.tensor_tensor(PTL[:, kb, :], R[2 + kb][:], PTH[:, kb, :].bitcast(fp32), ALU.subtract
                                        ).then_inc(pt_read, 1)

        cut_queries(0)
        maxima(0)
        for q in range(32):
            j, p = divmod(q, 4)
            denominators(q)
            if p == 3 and j < HP - 1:
                cut_queries(j + 1)
            if q < 31:
                maxima(q + 1)
            turned_rest(q)
            if p == 0:
                prepare(N_BG + j + 2)
            if p == 1:
                dve.wait_ge(gate_soft, j + 1)
                nc.vector.scalar_tensor_tensor(EV2[:], EV[:], 0.0, EV2[:], ALU.min, ALU.subtract
                                               ).then_inc(gate_log, 1)
            if j < HP - 1 and p == 2:
                dve.wait_ge(gate_silu, j + 1)
                for i in range(NU):
                    evacuate(NU * (N_BG + j + 1) + i, i, EV)
        dve.wait_ge(o_read, 32)
        for k in range(KT):
            dve.wait_ge((sg_in0, sg_in1)[k % 2], 16 * (k // 2 + 1))
            nc.vector.tensor_tensor(A[:, k, :], A[:, k, :], (EV, EV2)[k % 2][:], ALU.mult).then_inc(gated, 1)
            cut(k, 2)
        for m in range(KT):
            prepare(N_BO + m + 2)
            add_residual(N_BO + m, m, KT + m)
        dve.wait_ge(rb1_done, 2)
        for m in range(KT):
            nc.vector.scalar_tensor_tensor(A[:, m, :], A[:, m, :], gain[:, GAIN_F, m:m + 1], RB[:], ALU.mult, ALU.mult
                                           ).then_inc(y_done, 1)

    @block.tensor
    def _(pe):
        def unit(n, slot, i, first=False, split=None):
            if i == 0:
                pe.wait_ge(lo_done, n + 1)
            if not first:
                pe.wait_ge(unit_read, NU * n + i - 2)
            for k in range(KT):
                if split is not None:
                    pe.wait_ge(split, 2 * k + 2)
                for p, (w, x) in enumerate(((WH, XH), (WH, XL), (WL, XH))):
                    ins = nc.tensor.matmul(G[i][:, 0:TU], w[:, slot, k, :], x[:, k, seg(i)],
                                           start=(k == 0 and p == 0), stop=(k == KT - 1 and p == 2))
            ins.then_inc(unit_done, 1)

        def open_group(r, name):
            g = GINDEX[name] - NBANK_R
            if g >= 0:
                pe.wait_ge(*read_value(r, GROUPS[g][0]))
            else:
                last = max(x for x in range(NGROUP) if x % NBANK_R == GINDEX[name] % NBANK_R)
                sem, value = read_value(r - 1, GROUPS[last][0])
                pe.wait_ge(sem, value)
            return bank(name)

        def transposed(r, name, src, i):
            b = open_group(r, name)
            for c in range(4):
                ins = nc.tensor.transpose(b[:, c * P:(c + 1) * P], src[:, (4 * i + c) * P:(4 * i + c + 1) * P], ident[:])
            ins.then_inc(group_done, 1)

        def level(r, l):
            h = LEVELS[l]
            pe.wait_ge(level_done, NL * r + l + 1)
            b = open_group(r, f"L{h}")
            for c in range(NC):
                x = X[l % 3][:, c * P:(c + 1) * P]
                ins = nc.tensor.matmul(b[:, c * 64:(c + 1) * 64].rearrange("p (n h) -> p n h", h=h), x, upper(x, h),
                                       start=True, stop=True)
            ins.then_inc(group_done, 1)

        def recurrence(r, slot):
            if slot == 2:
                pe.wait_ge(k_done, r + 1)
                pe.wait_ge(q_done, r + 1)
                for i in range(2):
                    b = open_group(r, f"D{i}")
                    for c in range(4):
                        cols = slice((4 * i + c) * P, (4 * i + c + 1) * P)
                        ins = nc.tensor.matmul(b[:, c * P:(c + 1) * P], K[:, cols], Q[:, cols], start=True, stop=True)
                    ins.then_inc(group_done, 1)
                level(r, 0)
            if slot == 3:
                level(r, 1)
                level(r, 2)
            if slot == 4:
                level(r, 3)
            if slot == 5:
                level(r, 4)
                level(r, 5)
            if slot == 6:
                level(r, 6)
            if slot == 7:
                pe.wait_ge(ke_done, r + 1)
                for i in range(2):
                    transposed(r, f"T{i}", X[1], i)
            if slot == 8:
                pe.wait_ge(vd_done, r + 1)
                for i in range(2):
                    b = open_group(r, f"VB{i}")
                    nc.tensor.matmul(b[:], ones[:], X[0][:, half(i)], start=True, stop=True
                                     ).then_inc(group_done, 1)
                for i in range(2):
                    pe.wait_ge(*read_value(r, f"T{i}"))
                    b = open_group(r, f"S{i}")
                    for c in range(4):
                        ins = nc.tensor.matmul(b[:, c * P:(c + 1) * P], X[2][:, (4 * i + c) * P:(4 * i + c + 1) * P],
                                               VH[:, 4 * i + c, :], start=True, stop=True)
                    ins.then_inc(group_done, 1)

        def finish_head(r):
            pe.wait_ge(*read_value(r, "L1"))
            pe.wait_ge(qe_done, r + 1)
            for i in range(2):
                b = open_group(r, f"O{i}")
                for c in range(4 * i, 4 * i + 4):
                    cols = b[:, (c % 4) * P:(c % 4 + 1) * P]
                    ins = nc.tensor.matmul(cols, VH[:, c, :], AT[:, c, :], start=True, stop=(c == 0))
                    if c:
                        pe.wait_ge(st_step, NC * r + c)
                        ins = nc.tensor.matmul(cols, ST[:, c - 1, :], QE[:, c, :], start=False, stop=True)
                ins.then_inc(group_done, 1)
            pe.wait_ge(ss_done, r + 1)
            b = open_group(r, "OS")
            for n in range(DEC):
                ins = nc.tensor.matmul(b[:, n:n + 1], SS[:, n, :], Q[:, SEQ + n:SEQ + n + 1], start=True, stop=True)
            ins.then_inc(group_done, 1)
            pe.wait_ge(osq_done, r + 1)
            for i in range(NU):
                b = open_group(r, f"N{i}")
                nc.tensor.matmul(b[:, 0:TU], ones[:], X[0][:, seg(i)], start=True, stop=True).then_inc(group_done, 1)

        pe.wait_ge(setup_dve, 1)
        for k in range(KT):
            pe.wait_ge(sq_done, k + 1)
            for i in range(NU):
                ins = nc.tensor.matmul(R[i][:, 0:TU], ones[:], X[k % 3][:, seg(i)], start=(k == 0), stop=(k == KT - 1))
            ins.then_inc(sq_used, 1)

        def iteration(h, r):
            if r is not None:
                pe.wait_ge(unit_read, 9 * r + 3)
                for i in range(2):
                    transposed(r, f"VT{i}", RAWV, i)
            for slot in range(9):
                j, i = divmod(slot, 3)
                zero = type(h) is int and h == 0
                unit(3 * h + j, j, i, first=zero and j == 0, split=x_split if zero and slot == 0 else None)
                if r is not None:
                    recurrence(r, slot)
            if r is not None:
                finish_head(r)

        iteration(0, None)
        iteration(1, 0)
        with pe.Fori(2, HEADS) as h:
            iteration(h, h - 1)
        pe.wait_ge(unit_read, NU * N_G - 6)
        for i in range(2):
            transposed(HEADS - 1, f"VT{i}", RAWV, i)
        for slot in range(9):
            m, i = divmod(slot, 3)
            unit(N_G + m, (N_G + m) % 3, i)
            recurrence(HEADS - 1, slot)
        finish_head(HEADS - 1)
        for n in range(N_G + 3, N_AO):
            for i in range(NU):
                unit(n, n % 3, i)

        def first_block(n, stage):
            pe.wait_ge(lo_done, n + 1)
            for k in range(KT):
                pe.wait_ge(cut_lo, KT * stage + k + 1)
                for i in range(NU):
                    if k == 0:
                        pe.wait_ge(unit_read, NU * n + i - 2)
                    for p, (w, x) in enumerate(((WH, XH), (WH, XL), (WL, XH))):
                        ins = nc.tensor.matmul(G[i][:, 0:TU], w[:, n % 3, k, :], x[:, k, seg(i)],
                                               start=(k == 0 and p == 0), stop=(k == KT - 1 and p == 2))
                    if k == KT - 1:
                        ins.then_inc(unit_done, 1)

        def block_units(n):
            for i in range(NU):
                unit(n, n % 3, i)

        def sums(base):
            pe.wait_ge(sq1_added, base + KT)
            for i in range(NU):
                ins = nc.tensor.matmul(R[i][:, 0:TU], ones[:], SQA[:, seg(i)], start=True, stop=True)
            ins.then_inc(sums1_done, 1)

        first_block(N_AO, 0)
        for n in range(N_AO + 1, N_KV):
            block_units(n)
        first_block(N_KV, 1)
        sums(0)
        block_units(N_KV + 1)
        pe.wait_ge(unit_read, NU * N_BQ)
        for i in range(2):
            for c in range(4):
                ins = nc.tensor.transpose(R[3 + i][:, c * P:(c + 1) * P], RES[0][:, (4 * i + c) * P:(4 * i + c + 1) * P],
                                          ident[:])
            ins.then_inc(v_turned, 1)
        pe.wait_ge(rb1_done, 1)
        nc.tensor.transpose(R[2][0:DEC, 0:P], RES[0][:, SEQ:T], ident[:]).then_inc(v_turned, 1)
        for n in range(N_BQ, N_BG):
            block_units(n)
        unit(N_BG, N_BG % 3, 0)
        pe.wait_ge(d_qs, 1)
        pe.wait_ge(cache_in, 32)
        for b in range(DEC):
            nc.tensor.matmul(R[0][:, 16 * b:16 * b + 16], RES[0][:, b * P:(b + 1) * P],
                             QS[:, b].rearrange("p v j -> p (v j)"), start=True, stop=True)
        nc.tensor.matmul(R[1][:, 0:DEC], QS[:].rearrange("p b v j -> p (b v j)"), KSN[:], start=True, stop=True
                         ).then_inc(d_scores, 1)
        unit(N_BG, N_BG % 3, 1)
        pe.wait_ge(d_copied, 1)
        pe.wait_ge(vn_done, 1)
        nc.tensor.transpose(R[2][:, 0:P], SST[:], ident[:]).then_inc(d_turned, 1)
        unit(N_BG, N_BG % 3, 2)
        pe.wait_ge(d_prob, 1)
        nc.tensor.transpose(R[3][:, 0:P], SSN[:, 0:P], ident[:])
        nc.tensor.transpose(R[4][0:DEC, 0:P], SSN[:, P:], ident[:]).then_inc(d_ptur, 1)
        pe.wait_ge(d_pcop, 1)
        for b in range(DEC):
            cols = slice(16 * b, 16 * b + 16)
            nc.tensor.matmul(R[0][:, cols], RES[1][:, b * P:(b + 1) * P], PST[:, cols], start=True, stop=False)
            ins = nc.tensor.matmul(R[0][:, cols], VN[:], PSN[:, cols], start=False, stop=True)
        ins.then_inc(d_out, 1)

        def scores(q):
            nb, p = divmod(q, 4)
            keys = slice(P if nb == 0 else 0, 2 * P)
            tok = slice((nb - 1) * P + keys.start, (nb + 1) * P)
            if p == 0:
                pe.wait_ge(qn_done, nb + 1)
            for jj in range(2):
                if q:
                    pe.wait_ge(sc_read, 2 * (q - 1) + jj + 1)
                out = R[jj][:].rearrange("p (v w) -> p v w", v=2)[:, :, keys]
                for n, (a, k) in enumerate(((QNH, KBH), (QNH, KBL), (QNL, KBH))):
                    ins = nc.tensor.matmul(out, a[:, 2 * p + jj, :], k[:, :, tok], start=(n == 0), stop=(n == 2))
                ins.then_inc(sc_done, 1)

        def turn(q):
            pe.wait_ge(p_done, q + 1)
            for kb in range(1 if q < 4 else 0, 2):
                if q:
                    pe.wait_ge(pt_read, pt_count(q - 1, 1))
                for i in range(4):
                    ins = nc.tensor.transpose(R[2 + kb][:, i * P:(i + 1) * P], SP_[q % 2][:, i, kb * P:(kb + 1) * P],
                                              ident[:])
                ins.then_inc(pt_done, 1)

        def values(q):
            nb = q // 4
            kbs = range(1 if nb == 0 else 0, 2)
            pe.wait_ge(pt_read, pt_count(q, 1))
            if q:
                pe.wait_ge(o_read, q)
            steps = [(v, kb, a, b) for kb in kbs for v in range(2) for a, b in ((VPH, PTH), (VPH, PTL), (VPL, PTH))]
            for n, (v, kb, a, b) in enumerate(steps):
                ins = nc.tensor.matmul(R[4][:, 0:2 * P].rearrange("p (j w) -> p j w", j=2),
                                       a[:, nb - 1 + kb, 64 * v:64 * v + P],
                                       b[:, kb, :].rearrange("p (j v w) -> p j v w", j=2, v=2)[:, :, v, :],
                                       start=(n == 0), stop=(n == len(steps) - 1))
            ins.then_inc(pv_done, 1)

        pe.wait_ge(kb_done, 1)
        pe.wait_ge(vp_done, 2)
        pe.wait_ge(d_done, 1)
        scores(0)
        for q in range(32):
            j, p = divmod(q, 4)
            if q < 31:
                scores(q + 1)
            if j < HP - 1 and p < NU:
                unit(N_BG + j + 1, (N_BG + j + 1) % 3, p)
            turn(q)
            values(q)
        first_block(N_BO, 2)
        for n in range(N_BO + 1, NBLK):
            block_units(n)
        sums(KT)


def kernel(**inputs):
    import numpy as np
    from concourse import bacc
    from concourse.bass_utils import run_bass_kernel_spmd

    f = np.float32
    v = {k: np.asarray(a) for k, a in inputs.items()}

    def features_first(a):
        return a.reshape(KT, P, -1).transpose(1, 0, 2)

    x = np.concatenate([v["x_prompt"][0], v["x_sample"][:, 0]], 0).T
    pair = np.arange(16).reshape(2, HP).T.reshape(-1)
    qcols = (pair[:, None] * 64 + np.arange(64)).reshape(-1)

    def blocks(w):
        return w.reshape(KT, P, -1, P).transpose(2, 1, 0, 3)

    wa, wb = v["a_w_in"][0], v["b_w_in"][0]
    heads = np.stack([blocks(wa[:, c * D:(c + 1) * D]) for c in (2, 1, 0)], 1).reshape(3 * HEADS, P, KT, P)
    w = np.concatenate([heads, blocks(wa[:, 3 * D:]), blocks(v["a_w_out"][0]), blocks(v["w_kv"]),
                        blocks(wb[:, :D][:, qcols]), blocks(wb[:, D:][:, qcols]),
                        blocks(v["b_w_out"][0][qcols, :])], 0)
    fcol = lambda g: g.reshape(KT, P).T
    gains = np.stack([fcol(v["a_norm"][0]), np.broadcast_to(v["a_gnorm"][0][:, None], (P, KT)), fcol(v["kv_norm"]),
                      fcol(v["b_norm"][0]), fcol(v["final_norm"])], 1)
    tok = np.arange(P)
    lmask = np.zeros((P, NL, P // 2), f)
    for l, h in enumerate(LEVELS):
        n = np.repeat(np.arange(P // (2 * h)), h)
        lmask[:, l, :] = (tok[:, None] // (2 * h) == n[None]) & (tok[:, None] % (2 * h) < h)
    pos = np.concatenate([np.arange(SEQ), np.full(DEC, 4096)]).astype(f)
    inv = (f(1.0) / np.power(f(500000.0), np.arange(8, dtype=f) * f(2.0) / f(16.0), dtype=f)).astype(f)
    ang = (pos[None, :] * inv[:, None]).astype(f).astype(np.float64)
    cs = np.zeros((P, 2, T), f)
    cs[:, 0] = 1.0
    for b in (0, 64):
        cs[b:b + 8, 0] = cs[b + 8:b + 16, 0] = np.cos(ang)
        cs[b:b + 8, 1], cs[b + 8:b + 16, 1] = -np.sin(ang), np.sin(ang)
    rel = tok[:, None] + P - np.arange(2 * P)[None, :]
    amask = np.where((rel >= 0) & (rel <= P), 0.0, MASKED).astype(f)
    smask = np.where(tok[:, None] // 16 == np.arange(DEC)[None, :], 0.0, MASKED).astype(f)
    sk = v["b_sinks"][0][pair]
    arrays = {
        "x": features_first(x), "w": w, "gains": gains, "lbl": v["a_lb_logits"][0].reshape(HEADS, P).T,
        "states": v["state_hgrn"][0].transpose(1, 2, 0, 3), "lmask": lmask.reshape(P, -1),
        "ident": np.eye(P, dtype=f), "cs": cs, "amask": amask, "smask": smask,
        "sink": np.broadcast_to(sk, (P, 16)), "sinks": np.tile(v["b_sinks"][0], DEC)[:, None],
        "kc": v["cache_k_win"].transpose(2, 3, 0, 1).reshape(P, DEC, P),
        "vc": v["cache_v_win"].transpose(1, 0, 2, 3).reshape(P, DEC, P),
    }
    arrays = {k: np.ascontiguousarray(a) for k, a in arrays.items()}
    outs = {"y": (P, KT, T), "stp": (HEADS, P, P), "sts": (HEADS, P, DEC, P), "kwin": (P, P + DEC),
            "vwin": (P, P + DEC)}
    nc = bacc.Bacc("TRN2", target_bir_lowering=False, num_devices=1)
    ins = [nc.dram_tensor(k, a.shape, mybir.dt.from_np(a.dtype), kind="ExternalInput").ap() for k, a in arrays.items()]
    out = [nc.dram_tensor(k, sh, mybir.dt.float32, kind="ExternalOutput").ap() for k, sh in outs.items()]
    with ExitStack() as ctx:
        build(nc, ctx, ins, out)
    got = run_bass_kernel_spmd(nc, [arrays], core_ids=[0]).results[0]
    y = got["y"].transpose(2, 1, 0).reshape(T, D)
    kw, vw = (got[n].reshape(2, 64, P + DEC).transpose(2, 0, 1) for n in ("kwin", "vwin"))
    return (y[:SEQ][None], y[SEQ:][:, None], got["stp"][None, None], got["sts"].transpose(2, 0, 1, 3)[None],
            kw[:P][None], vw[:P][None], kw[P:][:, None], vw[P:][:, None])
```
